# Optimizing a Trainium2 kernel written in Bass

```python
import jax, jax.numpy as jnp
from jax import lax
import numpy as np

D_MODEL = 1024
BATCH = 1
SEQ = 128
DEPTH = 1
DEC_BATCH = 1
DEC_SEQ = 256
PAST_LEN = 128

GRID_W = 64
D_CONV = 512
CONV_W = 3
N_GLA_HEADS = 4
HEAD_DK = 128
HEAD_DV = 128
D_GLA_K = N_GLA_HEADS * HEAD_DK
D_GLA_V = N_GLA_HEADS * HEAD_DV
GLA_RANK = 16
GLA_GATE_NORM = 16.0
GLA_CHUNK = 64
N_EXPERTS = 64
TOP_K = 8
D_EXPERT = 256
D_SHARED = 256
ROUTED_SCALE = 2.5
EPS = 1e-6
SPLIT_SIZES = (D_CONV, D_CONV, D_CONV, D_GLA_K, D_GLA_K, D_GLA_V, D_GLA_V, GLA_RANK, GLA_RANK, D_MODEL, D_MODEL)
D_IN_PROJ = sum(SPLIT_SIZES)

kernel_name = "hybrid_diffusion_conv_gla_moe_step"

def rmsnorm(x, w):
    x32 = x.astype(jnp.float32)
    y = x32 * lax.rsqrt(jnp.mean(x32 * x32, axis=-1, keepdims=True) + EPS)
    return y.astype(x.dtype) * w

def conv3_rows(u, conv_w, conv_b, rows, row_len):
    bsz, l, ch = u.shape
    r = u.reshape(bsz, rows, row_len, ch)
    p = jnp.pad(r, ((0, 0), (0, 0), (1, 1), (0, 0)))
    y = (conv_w[0] * p[:, :, 0:row_len] + conv_w[1] * p[:, :, 1:row_len + 1]
         + conv_w[2] * p[:, :, 2:row_len + 2] + conv_b)
    return y.reshape(bsz, l, ch)

def gla_chunked(q, k, v, log_a, s0):
    bsz, nh, l, dk = q.shape
    dv = v.shape[-1]
    c = GLA_CHUNK
    n = l // c
    f32 = jnp.float32
    q = q.astype(f32).reshape(bsz, nh, n, c, dk)
    k = k.astype(f32).reshape(bsz, nh, n, c, dk)
    v = v.astype(f32).reshape(bsz, nh, n, c, dv)
    bcum = jnp.cumsum(log_a.astype(f32).reshape(bsz, nh, n, c, dk), axis=3)
    mask = jnp.tril(jnp.ones((c, c), dtype=bool))
    diff = bcum[:, :, :, :, None, :] - bcum[:, :, :, None, :, :]
    decay = jnp.exp(jnp.where(mask[:, :, None], diff, -jnp.inf))
    scores = jnp.sum(q[:, :, :, :, None, :] * k[:, :, :, None, :, :] * decay, axis=-1)
    o_intra = jnp.einsum('bhnij,bhnje->bhnie', scores, v)
    b_last = bcum[:, :, :, -1, :]
    k_tail = k * jnp.exp(b_last[:, :, :, None, :] - bcum)
    u = jnp.einsum('bhncd,bhnce->bhnde', k_tail, v)
    a_chunk = jnp.exp(b_last)

    def step(s, inp):
        a, uu = inp
        return a[..., None] * s + uu, s

    s_final, s_starts = lax.scan(step, s0.astype(f32),
                                 (jnp.moveaxis(a_chunk, 2, 0), jnp.moveaxis(u, 2, 0)))
    s_starts = jnp.moveaxis(s_starts, 0, 2)
    o_inter = jnp.einsum('bhncd,bhnde->bhnce', q * jnp.exp(bcum), s_starts)
    o = (o_intra + o_inter).reshape(bsz, nh, l, dv)
    return o, s_final

def to_heads(t, hd):
    bsz, l, _ = t.shape
    return t.reshape(bsz, l, N_GLA_HEADS, hd).transpose(0, 2, 1, 3)

def gla_mixer(q, k, v, g_out, lr_f, lr_b, w_decay, b_decay, gla_norm_w, s0_f, s0_b):
    bsz, l, _ = q.shape
    qh = to_heads(q, HEAD_DK) * (HEAD_DK ** -0.5)
    kh = to_heads(k, HEAD_DK)
    vh = to_heads(v, HEAD_DV)
    la_f = to_heads(jax.nn.log_sigmoid((lr_f @ w_decay[0] + b_decay[0]).astype(jnp.float32)) / GLA_GATE_NORM, HEAD_DK)
    la_b = to_heads(jax.nn.log_sigmoid((lr_b @ w_decay[1] + b_decay[1]).astype(jnp.float32)) / GLA_GATE_NORM, HEAD_DK)
    o_f, s_f = gla_chunked(qh, kh, vh, la_f, s0_f)
    flip = lambda t: jnp.flip(t, axis=2)
    o_b, s_b = gla_chunked(flip(qh), flip(kh), flip(vh), flip(la_b), s0_b)
    o = o_f + flip(o_b)
    o = o * lax.rsqrt(jnp.mean(o * o, axis=-1, keepdims=True) + EPS)
    o = o.astype(q.dtype) * gla_norm_w[None, :, None, :]
    o = o.transpose(0, 2, 1, 3).reshape(bsz, l, D_GLA_V)
    return o * jax.nn.silu(g_out), s_f.astype(q.dtype), s_b.astype(q.dtype)

def moe(h, w_router, b_router, w_gate_e, w_up_e, w_down_e, w_gate_s, w_up_s, w_down_s):
    bsz, l, d = h.shape
    t = h.reshape(bsz * l, d)
    scores = jax.nn.sigmoid((t @ w_router).astype(jnp.float32))
    _, idx = lax.top_k(scores + b_router.astype(jnp.float32), TOP_K)
    sel = jnp.take_along_axis(scores, idx, axis=-1)
    wts = sel / jnp.sum(sel, axis=-1, keepdims=True) * ROUTED_SCALE
    combine = jnp.sum(jax.nn.one_hot(idx, N_EXPERTS, dtype=jnp.float32) * wts[..., None], axis=1)
    hg = jnp.einsum('td,edf->tef', t, w_gate_e)
    hu = jnp.einsum('td,edf->tef', t, w_up_e)
    act = jax.nn.silu(hg) * hu * combine[..., None].astype(t.dtype)
    routed = jnp.einsum('tef,efd->td', act, w_down_e)
    shared = (jax.nn.silu(t @ w_gate_s) * (t @ w_up_s)) @ w_down_s
    return (routed + shared).reshape(bsz, l, d)

def trunk_layer(x, cond, rows, row_len, s0_f, s0_b, p):
    (w_mod, b_mod, norm1_w, w_in, conv_w, conv_b, w_decay, b_decay, gla_norm_w,
     w_br_conv, w_br_gla, w_out, norm2_w, w_router, b_router,
     w_gate_e, w_up_e, w_down_e, w_gate_s, w_up_s, w_down_s) = p
    mod = (jax.nn.silu(cond) @ w_mod + b_mod)[:, None, :]
    sh1, sc1, g1, sh2, sc2, g2 = jnp.split(mod, 6, axis=-1)
    h = rmsnorm(x, norm1_w) * (1 + sc1) + sh1
    points = np.cumsum(SPLIT_SIZES)[:-1].tolist()
    (u_in, gate_b, gate_c, q, k, v, g_out, lr_f, lr_b,
     gate_br_conv, gate_br_gla) = jnp.split(h @ w_in, points, axis=-1)
    y_conv = gate_b * conv3_rows(gate_c * u_in, conv_w, conv_b, rows, row_len)
    y_gla, s_f, s_b = gla_mixer(q, k, v, g_out, lr_f, lr_b, w_decay, b_decay, gla_norm_w, s0_f, s0_b)
    merged = (jax.nn.sigmoid(gate_br_conv) * (y_conv @ w_br_conv)
              + jax.nn.sigmoid(gate_br_gla) * (y_gla @ w_br_gla))
    x = x + g1 * (merged @ w_out)
    h2 = rmsnorm(x, norm2_w) * (1 + sc2) + sh2
    x = x + g2 * moe(h2, w_router, b_router, w_gate_e, w_up_e, w_down_e, w_gate_s, w_up_s, w_down_s)
    return x, s_f, s_b

def setup_inputs(seed: int = 0) -> dict:
    key = jax.random.key(seed)
    ks = jax.random.split(key, 32)
    nrm = lambda i, shape, s: jax.random.normal(ks[i], shape, jnp.float32) * s
    L = DEPTH
    return {
        "x_prompt": nrm(0, (BATCH, SEQ, D_MODEL), 1.0),
        "x_sample": nrm(1, (DEC_BATCH, DEC_SEQ, D_MODEL), 1.0),
        "state_gla": nrm(2, (DEC_BATCH, DEPTH, 2, N_GLA_HEADS, HEAD_DK, HEAD_DV), 0.5),
        "c": nrm(3, (DEC_BATCH, D_MODEL), 1.0),
        "c_ctx": nrm(4, (D_MODEL,), 1.0),
        "w_mod": nrm(5, (L, D_MODEL, 6 * D_MODEL), 0.5 * D_MODEL ** -0.5),
        "b_mod": nrm(6, (L, 6 * D_MODEL), 0.02),
        "norm1_w": 1.0 + nrm(7, (L, D_MODEL), 0.02),
        "w_in": nrm(8, (L, D_MODEL, D_IN_PROJ), D_MODEL ** -0.5),
        "conv_w": nrm(9, (L, CONV_W, D_CONV), CONV_W ** -0.5),
        "conv_b": nrm(10, (L, D_CONV), 0.02),
        "w_decay": nrm(11, (L, 2, GLA_RANK, D_GLA_K), GLA_RANK ** -0.5),
        "b_decay": nrm(12, (L, 2, D_GLA_K), 0.1),
        "gla_norm_w": 1.0 + nrm(13, (L, N_GLA_HEADS, HEAD_DV), 0.02),
        "w_br_conv": nrm(14, (L, D_CONV, D_MODEL), D_CONV ** -0.5),
        "w_br_gla": nrm(15, (L, D_GLA_V, D_MODEL), D_GLA_V ** -0.5),
        "w_out": nrm(16, (L, D_MODEL, D_MODEL), D_MODEL ** -0.5),
        "norm2_w": 1.0 + nrm(17, (L, D_MODEL), 0.02),
        "w_router": nrm(18, (L, D_MODEL, N_EXPERTS), D_MODEL ** -0.5),
        "b_router": nrm(19, (L, N_EXPERTS), 0.01),
        "w_gate_e": nrm(20, (L, N_EXPERTS, D_MODEL, D_EXPERT), D_MODEL ** -0.5),
        "w_up_e": nrm(21, (L, N_EXPERTS, D_MODEL, D_EXPERT), D_MODEL ** -0.5),
        "w_down_e": nrm(22, (L, N_EXPERTS, D_EXPERT, D_MODEL), D_EXPERT ** -0.5),
        "w_gate_s": nrm(23, (L, D_MODEL, D_SHARED), D_MODEL ** -0.5),
        "w_up_s": nrm(24, (L, D_MODEL, D_SHARED), D_MODEL ** -0.5),
        "w_down_s": nrm(25, (L, D_SHARED, D_MODEL), D_SHARED ** -0.5),
        "final_norm_w": 1.0 + nrm(26, (D_MODEL,), 0.02),
    }

def reference(x_prompt, x_sample, state_gla, c, c_ctx, w_mod, b_mod, norm1_w, w_in, conv_w, conv_b,
              w_decay, b_decay, gla_norm_w, w_br_conv, w_br_gla, w_out, norm2_w, w_router, b_router,
              w_gate_e, w_up_e, w_down_e, w_gate_s, w_up_s, w_down_s, final_norm_w):
    y_p = x_prompt
    y_s = x_sample
    ctx_len = x_prompt.shape[1]
    rows = x_sample.shape[1] // GRID_W
    s_zero = jnp.zeros((x_prompt.shape[0], N_GLA_HEADS, HEAD_DK, HEAD_DV), x_prompt.dtype)
    ctx_cond = c_ctx[None, :]
    new_states = []
    for l in range(DEPTH):
        p = (w_mod[l], b_mod[l], norm1_w[l], w_in[l], conv_w[l], conv_b[l], w_decay[l], b_decay[l],
             gla_norm_w[l], w_br_conv[l], w_br_gla[l], w_out[l], norm2_w[l], w_router[l], b_router[l],
             w_gate_e[l], w_up_e[l], w_down_e[l], w_gate_s[l], w_up_s[l], w_down_s[l])
        y_p, s_f, s_b = trunk_layer(y_p, ctx_cond, 1, ctx_len, s_zero, s_zero, p)
        new_states.append(jnp.stack([s_f, s_b], axis=1))
        y_s, _, _ = trunk_layer(y_s, c, rows, GRID_W, state_gla[:, l, 0], state_gla[:, l, 1], p)
    new_state_gla = jnp.stack(new_states, axis=1)
    y_prompt = rmsnorm(y_p, final_norm_w)
    y_sample = rmsnorm(y_s, final_norm_w)
    return (y_prompt, y_sample, new_state_gla)


_drawn_inputs = setup_inputs


def setup_inputs(seed=0):
    import zlib

    import numpy as np

    out = dict(_drawn_inputs(seed))
    spreads = {}
    factors = {'state_gla': 7.984,
     'conv_b': 21.588,
     'gla_norm_w': 17.115,
     'final_norm_w': 21.423,
     'norm2_w': 4.194}
    for name, (base, spread) in spreads.items():
        noise = np.random.default_rng([zlib.crc32(name.encode()), seed]).standard_normal(out[name].shape)
        drawn = base * np.exp(spread * noise) if base else spread * noise
        out[name] = __import__('jax').numpy.asarray(drawn.astype(out[name].dtype))
    for name, factor in factors.items():
        out[name] = (out[name] * factor).astype(out[name].dtype)
    return out
```

```python
from contextlib import ExitStack

import concourse.bass as bass
from concourse import mybir

F32 = mybir.dt.float32
BF16 = mybir.dt.bfloat16
I32 = mybir.dt.int32
U8 = mybir.dt.uint8
ALU = mybir.AluOpType
ACT = mybir.ActivationFunctionType
AX = mybir.AxisListType

P = 128
D = 1024
KT = D // P
CTX = 128
LAT = 256
TOK = CTX + LAT
NT = TOK // P
SEQ_OF = [0, 1, 1]
SLOTS = 96
GRID = 64
DC = 512
CT = DC // P
NH = 4
CHUNK = 64
NCH = TOK // CHUNK
RANK = 16
GATE_NORM = 16.0
NE = 64
TOPK = 8
DE = 256
ROUTED_SCALE = 2.5
EPS = 1e-6
CLAMP = 80.0 * GATE_NORM

C_U, C_GB, C_GC, C_Q, C_K, C_V, C_GO, C_LR = (512 * i for i in range(8))
C_GBC = C_LR + 2 * RANK
C_GBG = C_GBC + D

UNITS = 5
UNIT = 2048
NXS = 4
FAR = 8192.0

SCAN = {0: [0, 1, 2, 3, 4, 5], 1: [1, 0, 5, 4, 3, 2]}
LAST = {0: CHUNK - 1, 1: 0}
MID = {0: CHUNK // 2 - 1, 1: CHUNK // 2}


def plan_units():
    units = [("mod", 0, k) for k in range(KT)]
    for name in ("u", "gc", "gb", "k", "q", "v", "go"):
        units += [(name, i) for i in range(2)]
    for name in ("gbc", "gbg"):
        units += [(name, i) for i in range(4)]
    for g in (1, 2):
        units += [("mod", g, k) for k in range(KT)]
    units += [("wbc", 0), ("wbg", 0), ("wbc", 1), ("wbg", 1)]
    units += [("wo", i) for i in range(4)]
    return units


def plan_jobs():
    jobs = [("mod", 0), ("modT",), ("cols",)]
    jobs += [("xT", k) for k in range(KT)]
    jobs += [("lr",)] + [("z", d, h) for d in range(2) for h in range(NH)]
    for name in ("u", "gc", "gb", "k", "q"):
        jobs += [(name, c) for c in range(CT)]
    jobs += [("v", t) for t in range(NT)]
    jobs += [("go", c) for c in range(CT)]
    jobs += [("kt", d, h) for d in range(2) for h in range(NH)]
    for h in range(NH):
        jobs += [("sc", d, h) for d in range(2)]
        jobs += [("up", d, h, i) for d in range(2) for i in range(2)]
        jobs += [("o", h)]
        if h:
            jobs += [("ss", h - 1)]
    jobs += [("ss", NH - 1)]
    jobs += [("gbc", n) for n in range(KT)] + [("gbg", n) for n in range(KT)]
    for g in (1, 2):
        jobs += [("mod", g)]
    jobs += [("bg1", s, i) for s in range(2) for i in range(2)]
    for n in range(KT):
        jobs += [("mc", n), ("mg", n)]
    jobs += [("out", i, t) for i in range(2) for t in range(NT)]
    jobs += [("bg2", s, i) for s in range(2) for i in range(2)]
    for s in range(2):
        for i in range(2):
            jobs += [("ba", s, i), ("bb", s, i)]
    jobs += [("h2T", k) for k in range(KT)]
    jobs += [("r", t) for t in range(NT)]
    jobs += [("sgu", t) for t in range(NT)]
    jobs += [("pos", t) for t in range(NT)] + [("cnt",)]
    jobs += [("shT", t) for t in range(NT)]
    jobs += [("sy", t, i) for t in range(NT) for i in range(2)]
    return jobs


def program(nc, x_prompt, x_sample, state_gla, c, c_ctx, w_mod, b_mod, norm1_w, w_in, conv_w, conv_b,
            w_decay, b_decay, gla_norm_w, w_br_conv, w_br_gla, w_out, norm2_w, w_router, b_router,
            w_gate_e, w_up_e, w_down_e, w_gate_s, w_up_s, w_down_s, final_norm_w,
            y_prompt, y_sample, new_state):
    units = plan_units()
    unit_at = {u: n for n, u in enumerate(units)}
    jobs = plan_jobs()
    bank_of = {j: n % 8 for n, j in enumerate(jobs)}
    turn_of = {j: n // 8 for n, j in enumerate(jobs)}

    h2_dram = nc.dram_tensor("h2_rows", [TOK, D], F32).ap()
    rows_dram = nc.dram_tensor("expert_rows", [TOK * TOPK, D], F32).ap()

    with ExitStack() as ctx:
        def sem(name):
            return ctx.enter_context(nc.semaphore(name))

        SIZE = 53200
        arena = ctx.enter_context(nc.sbuf_tensor("arena", [P, SIZE], F32))
        banks = [ctx.enter_context(nc.psum_tensor(f"bank{i}", [P, 512], F32)) for i in range(8)]
        top = [0]

        def take(n):
            a = top[0]
            top[0] += n
            assert top[0] <= SIZE, (top[0], SIZE)
            return a

        def at(a, *shape):
            n = 1
            for s in shape:
                n *= s
            v = arena[:, a:a + n]
            if len(shape) == 2:
                return v.rearrange("p (a b) -> p a b", b=shape[1])
            if len(shape) == 3:
                return v.rearrange("p (a b c) -> p a b c", b=shape[1], c=shape[2])
            if len(shape) == 4:
                return v.rearrange("p (a b c d) -> p a b c d", b=shape[1], c=shape[2], d=shape[3])
            return v

        a_ring = take(UNITS * UNIT)
        ring = at(a_ring, UNITS, UNIT)
        a_mix = take(3 * 1536 + 40)
        conv_rows = CTX + 2 + (LAT // GRID) * (GRID + 2)
        u_sb = at(a_mix, CT, TOK)
        gated_u = at(a_mix + 1536, CT, conv_rows)
        gb_sb = at(a_mix + 1536 + CT * conv_rows, CT, TOK)
        kT = at(a_mix, NH, TOK)
        qT = at(a_mix + 1536, NH, TOK)
        v_sb = at(a_mix + 3072, NT, DC)
        merged = at(a_mix, KT, TOK)
        y_conv = at(take(1536), CT, TOK)
        y_gla = at(take(1536), NH, TOK)
        rms_o = at(take(1536), NH, TOK)
        squares = at(take(768), 2, TOK)
        conv_acc = at(take(conv_rows), conv_rows)
        a_s0 = take(1024)
        state0 = at(a_s0, 2 * NH, P)
        new_st = at(take(1024), 2 * NH, P)
        a_st = take(4 * TOK)
        masked = at(a_st, 2, 2, TOK)
        take(NXS * 3 * UNIT - top[0])
        expert_w = at(0, NXS, 3 * UNIT)

        a_decay = take(3072)
        zz = at(a_decay, 2, NH, TOK)
        k_tail = at(a_decay, 2, NH, TOK)
        a_cum = take(3072)
        cum = at(a_cum, 2, NH, TOK)
        x1 = at(a_cum, NT, D)
        a_fac = take(9216)
        tail_f = at(a_fac, 2, NH, TOK)
        key_f = at(a_fac + 3072, 2, NH, TOK)
        qry_f = at(a_fac + 6144, 2, NH, TOK)
        g_conv = at(a_fac, KT, TOK)
        g_gla = at(a_fac + 3072, KT, TOK)
        shared_w = at(a_fac, 3, UNIT)
        h2 = at(a_fac + 6144, NT, D)
        a_hT = take(3072)
        hT = at(a_hT, KT, TOK)
        a_x = take(4096)
        xn = at(a_x, NT, D)
        states = at(a_x, 2 * NH, 4, P)
        tmp = at(a_x, 2, 512)
        junk = at(a_x + 1024, D)
        g1_rows = at(a_decay, 2, D)
        g2_rows = at(take(2048), 2, D)
        a_rows = take(1536)
        mod_rows = at(a_rows, 3, 512)
        wd = at(a_fac, 2, DC)
        lrT = at(a_fac + 1024, TOK)
        lrw = at(a_fac + 1024 + TOK, KT, 2 * RANK)
        norm2_rows = at(a_fac + 6144, 512)
        wr = at(take(512), KT, NE)

        def score_tile(n):
            return at(a_x + 3 * NE * n, NT, NE)

        scores, biased, rest, chosen, weight, rank, part = (score_tile(n) for n in range(7))
        top8 = at(a_x + 3 * NE * 7, NT, 8)
        weight_sum = at(a_x + 3 * NE * 7 + 24, NT)
        table = at(a_x, NE, 8)
        act_s = at(a_x + 2048, NT, DE)
        actT_s = at(a_x + 2048 + 768, NT, DE)
        y_shared = h2
        last_w = at(a_hT, D)
        onehot = arena[:, a_decay:a_decay + 1536].bitcast(BF16).rearrange("p (b t e s) -> p b t e s", b=2, t=NT, e=4)
        x_g = [at(a, D) for a in (a_x, a_x + D, a_hT + D, a_hT + 2 * D)]
        x_T = at(a_x + 2048, 2, KT, P)
        y_e = [at(a, D) for a in (a_decay, a_decay + D, a_fac + D, a_fac + 2 * D)]
        actT_e = at(a_decay + 2560, 2, DE)
        vals = arena[:, a_rows:a_rows + 768].bitcast(BF16).rearrange("p (t e v) -> p t e v", t=NT, v=8)
        gather_f = at(a_rows + 768, NE)
        gather_i = gather_f.bitcast(I32)
        scatter_f = at(a_rows + 832, NE)
        scatter_i = scatter_f.bitcast(I32)
        wt = at(a_rows + 896, NE)
        place = at(a_rows + 960, NT, NE)
        place_b = at(a_rows + 1152, NT, NE)
        iota_f = at(a_rows + 1344, P)
        most_f = at(a_rows + 1472, 1)
        most_i = at(a_rows + 1473, 1).bitcast(I32)
        current = at(a_rows + 1474, 8).bitcast(I32)
        sil_e = at(a_fac, 2, DE)
        iota_i = at(take(P), P).bitcast(I32)
        part_i = at(take(1), 1).bitcast(I32)
        part_f = at(take(1), 1)
        before = arena[:, take(64):top[0]].bitcast(BF16)
        ones_b = arena[:, take(64):top[0]].bitcast(BF16)
        chosen_b = arena[:, take(96):top[0]].bitcast(BF16).rearrange("p (t e) -> p t e", t=NT)
        router_b = at(take(NE), NE)

        ident = at(take(P), P)
        ones = at(take(P), P)
        sel = at(take(2 * P), 2, P)
        eye32 = at(take(32), 32)
        restart = at(take(TOK), TOK)
        mask = [arena[:, a:a + TOK // 4].bitcast(U8) for a in (take(TOK // 4), take(TOK // 4))]
        rows_in = at(take(P), P)
        cols = at(take(44), 44)
        modT = at(take(96), 4, 4, 2)
        scale1 = at(take(16), KT, 2)
        scond = at(take(16), 2, KT)
        total = at(take(24), 24)
        a_last = at(take(48), 2, 24)
        stat = at(take(16), 16)
        stat2 = at(take(16), 16)

        sem_names = ("shared_in chosen_ready tokens_ready moe_done norm_w_in rows_in routed_ready final_sq final_sqrt final_ready ssil_ready state_done out_done zeroed scale_ready norm2_in small_in x_in state_in wd_in lr_in mod_b_in router_in x_again_in "
                     "act_chain dve_chain pool_chain mod_unit_used "
                     "consts cond_ready sumsq xn_ready mod_ready rstd_ready "
                     "abs_ready log_ready cum_ready last_ready exp_ready fac_ready conv_done "
                     "sq_ready ro_ready sqrt_ready gla_ready merged_ready x1_ready "
                     "x1_sq x1_sqrt h2_ready h2_out").split()
        S = {n: sem(n) for n in sem_names}
        unit_in = [sem(f"unit_in{i}") for i in range(UNITS)]
        bank_full = [sem(f"bank_full{i}") for i in range(8)]
        bank_free = [sem(f"bank_free{i}") for i in range(8)]

        def bank(job):
            return banks[bank_of[job]]

        def full(eng, job):
            eng.wait_ge(bank_full[bank_of[job]], turn_of[job] + 1)

        def drained(eng, job):
            eng.wait_ge(bank_free[bank_of[job]], turn_of[job] + 1)

        def free(ins, job):
            ins.then_inc(bank_free[bank_of[job]], 1)

        w_in0, w_mod0 = w_in[0], w_mod[0]
        w_in_col = {"u": C_U, "gb": C_GB, "gc": C_GC, "q": C_Q, "k": C_K, "v": C_V, "go": C_GO,
                    "gbc": C_GBC, "gbg": C_GBG}

        def last_job(u):
            if u[0] == "mod":
                return ("mod", u[1])
            if u[0] in ("wbc", "wbg"):
                return ("m" + u[0][2], 4 * u[1] + 3)
            if u[0] == "wo":
                return ("out", u[1] // 2, NT - 1)
            if u[0] == "v":
                return ("v", NT - 1)
            return (u[0], 2 * u[1] + 1)

        def unit_source(u):
            if u[0] == "mod":
                return w_mod0[:, u[1] * 2048:(u[1] + 1) * 2048].rearrange("(p k) n -> k p n", k=KT)[u[2]]
            if u[0] in ("wbc", "wbg"):
                w = (w_br_conv if u[0] == "wbc" else w_br_gla)[0]
                return w[:, u[1] * 512:(u[1] + 1) * 512].rearrange("(k p) n -> p k n", p=P)
            if u[0] == "wo":
                return w_out[0][:, u[1] * 256:(u[1] + 1) * 256].rearrange("(k p) n -> p k n", p=P)
            c0 = w_in_col[u[0]] + 256 * u[1]
            return w_in0[:, c0:c0 + 256].rearrange("(k p) n -> p k n", p=P)

        def unit_view(u):
            n = unit_at[u]
            v = ring[:, n % UNITS, :]
            if u[0] == "mod":
                return v
            if u[0] in ("wbc", "wbg"):
                return v.rearrange("p (k n) -> p k n", k=4)
            return v.rearrange("p (k n) -> p k n", k=KT)

        rows_all = arena[:, 0:NT * TOPK * D].rearrange("p (t k d) -> p t k d", t=NT, k=TOPK)
        rows_in_sem = [sem(f"rows_in{t}") for t in range(NT)]
        ex_names = ("table_full table_free onehot_done onehot_used index_ready xtr_done xT_a xT_b gu_done sil_done "
                    "act_done y_done y_a y_b index_copied index_seen rows_free dve_chain").split()
        X = []
        for n in range(2):
            d = {k: sem(f"{k}_{n}") for k in ex_names}
            for k, m in (("w_in", NXS), ("gathered", 4), ("scattered", 4)):
                d[k] = [sem(f"{k}{i}_{n}") for i in range(m)]
            X.append(d)

        def load_expert(eng, x, e, u):
            for n, w in enumerate((w_gate_e, w_up_e)):
                eng.dma_start(expert_w[:, u, UNIT * n:UNIT * n + UNIT].rearrange("p (k f) -> p k f", k=KT),
                              w[0, bass.ds(e, 1)].rearrange("a (k p) f -> p (a k) f", p=P)).then_inc(x["w_in"][u], 16)
            eng.dma_start(expert_w[:, u, 2 * UNIT:3 * UNIT].rearrange("p (k n) -> p k n", k=2),
                          w_down_e[0, bass.ds(e, 1)].rearrange("a (k p) n -> p (a k) n", p=P)).then_inc(x["w_in"][u], 16)

        def is_first(e):
            return isinstance(e, int) and e == 0

        def is_second(e):
            return isinstance(e, int) and e == 1

        def earlier_in(n, e, u, each):
            return (e - u % n) * (each // n)

        def spill(eng, body):
            eng.wait_ge(S["tokens_ready"], 1)
            most = eng.value_load(most_i[0:1, 0:1], min_val=0, max_val=TOK)
            for c in range(1, TOK // SLOTS):
                with eng.If(most > SLOTS * c):
                    body(eng, X[1], c)


        def sp_spill(sp, x, c):
            sp.wait_ge(X[0]["y_done"], NE)
            with sp.Fori(0, NE) as e:
                sp.wait_ge(x["y_done"], e + (1 + NE * (c - 1)))
                load_expert(sp, x, e, 0)

        def pool_spill(pool, x, c):
            pool.wait_ge(x["index_ready"], c)
            if c == 1:
                pool.sem_inc(x["rows_free"], 1)
            with pool.Fori(0, NE) as e:
                n = e + NE * (c - 1)
                pool.wait_ge(x["xtr_done"], n + 1)
                pool.tensor_copy(current[:, 0:1], gather_i[:, bass.ds(e, 1)]).then_inc(x["index_copied"], 1)
                gather_rows(pool, x, 0, 2 * n + 1)
                pool.wait_ge(x["y_a"], n + 2)
                pool.wait_ge(x["y_b"], n + 2)
                pool.tensor_copy(current[:, 4:5], scatter_i[:, bass.ds(e, 1)]).then_inc(x["index_copied"], 1)
                scatter_rows(pool, x, 0, 2 * n + 2)
                pool.wait_ge(x["scattered"][0], 16 * n + 16)
                pool.sem_inc(x["rows_free"], 1)

        def pe_spill(pe, x, c):
            if c == 1:
                pe.wait_ge(X[0]["y_a"], NE)
                pe.wait_ge(X[0]["y_b"], NE)
                pe.sem_inc(x["xtr_done"], 1)
                pe.sem_inc(x["y_done"], 1)
            pe_tables(pe, x, c - 1)
            with pe.Fori(0, NE) as e:
                n = e + NE * (c - 1)
                pe.wait_ge(x["gathered"][0], 16 * n + 16)
                pe.wait_ge(x["xT_a"], n + 1)
                pe.wait_ge(x["xT_b"], n + 1)
                rows_to_features(pe, 0).then_inc(x["xtr_done"], 1)
                pe.wait_ge(x["w_in"][0], 48 * n + 48)
                pe.wait_ge(x["xT_a"], n + 2)
                pe.wait_ge(x["xT_b"], n + 2)
                gate_up_products(pe, 0, 0).then_inc(x["gu_done"], 1)
                pe.wait_ge(x["act_done"], n + 1)
                pe.wait_ge(x["y_a"], n + 1)
                pe.wait_ge(x["y_b"], n + 1)
                down_products(pe, 0, 0).then_inc(x["y_done"], 1)

        def act_spill(act, x, c):
            if c == 1:
                act.sem_inc(x["xT_b"], 1)
                act.sem_inc(x["y_b"], 1)
            with act.Fori(0, NE) as e:
                n = e + NE * (c - 1)
                act.wait_ge(x["xtr_done"], n + 2)
                act.activation(x_T[:, 0, 4:8, 0:SLOTS], x_copy_source(1), ACT.Copy)\
                    .then_inc(x["xT_b"], 1)
                act.wait_ge(x["gu_done"], n + 1)
                silu_of(act, 0).then_inc(x["sil_done"], 1)
                act.wait_ge(x["y_done"], n + 2)
                act.wait_ge(x["rows_free"], n + 1)
                weighted_b(act, 0, e).then_inc(x["y_b"], 1)

        def dve_spill(dve, x, c):
            if c == 1:
                for b in range(4):
                    dve.wait_ge(X[0]["scattered"][b], 16 * NE // 4)
                dve.sem_inc(x["xT_a"], 1)
                dve.sem_inc(x["y_a"], 1)
            else:
                dve.wait_ge(x["rows_free"], NE * (c - 1) + 1)
            def link(ins):
                chain["count"] += 1
                ins.then_inc(x["dve_chain"], 1)
                dve.wait_ge(x["dve_chain"], chain["count"])

            link(dve.tensor_scalar(place, place, -float(SLOTS), None, ALU.add))
            dve_tables(dve, link, x, c - 1)
            with dve.Fori(0, NE) as e:
                n = e + NE * (c - 1)
                dve.wait_ge(x["xtr_done"], n + 2)
                dve.tensor_copy(x_T[:, 0, 0:4, 0:SLOTS], x_copy_source(0)).then_inc(x["xT_a"], 1)
                dve.wait_ge(x["sil_done"], n + 1)
                silu_product(dve, 0).then_inc(x["act_done"], 1)
                dve.wait_ge(x["y_done"], n + 2)
                dve.wait_ge(x["rows_free"], n + 1)
                weighted_a(dve, 0, e).then_inc(x["y_a"], 1)

        def gather_rows(pool, x, b, copied):
            pool.wait_ge(x["index_copied"], copied)
            pool.sem_inc(x["index_seen"], 1)
            pool.indirect_dma_start(out=x_g[b][0:SLOTS, :], out_offset=None, in_=h2_dram,
                                    in_offset=bass.IndirectOffsetOnAxis(ap=current[0:SLOTS, b:b + 1], axis=0),
                                    bounds_check=bound["gather"], oob_is_err=False).then_inc(x["gathered"][b], 16)

        def scatter_rows(pool, x, b, copied):
            pool.wait_ge(x["index_copied"], copied)
            pool.sem_inc(x["index_seen"], 1)
            pool.indirect_dma_start(out=rows_dram,
                                    out_offset=bass.IndirectOffsetOnAxis(ap=current[0:SLOTS, 4 + b:5 + b], axis=0),
                                    in_=y_e[b][0:SLOTS, :], in_offset=None,
                                    bounds_check=bound["scatter"], oob_is_err=False).then_inc(x["scattered"][b], 16)

        bound, chain = {}, {"count": 0}

        def rows_to_features(pe, b):
            for k in range(KT):
                ins = pe.transpose(banks[k // 4][:, P * (k % 4):P * (k % 4) + SLOTS],
                                   x_g[b][0:SLOTS, P * k:P * k + P], ident[0:SLOTS, 0:SLOTS])
            return ins

        def gate_up_products(pe, b, u):
            w = expert_w[:, u, 0:2 * UNIT].rearrange("p (m k f) -> p m k f", m=2, f=DE)
            for m in range(2):
                for f in range(2):
                    c = P * (2 * m + f)
                    for k in range(KT):
                        ins = pe.matmul(banks[2 + b][:, c:c + SLOTS], w[:, m, k, P * f:P * f + P],
                                        x_T[:, b, k, 0:SLOTS], start=(k == 0), stop=(k == KT - 1))
            return ins

        def down_products(pe, b, u):
            w = expert_w[:, u, 2 * UNIT:3 * UNIT].rearrange("p (k n) -> p k n", k=2)
            for k in range(2):
                for i in range(2):
                    ins = pe.matmul(banks[5 + i][0:SLOTS, :], actT_e[:, b, P * k:P * k + SLOTS],
                                    w[:, k, 512 * i:512 * i + 512], start=(k == 0), stop=(k == 1))
            return ins

        def blocks(a):
            return a.rearrange("p (k s) -> p k s", s=P)[:, :, 0:SLOTS]

        def x_copy_source(i):
            return blocks(banks[i][:, :])

        def silu_product(dve, b):
            return dve.tensor_tensor(blocks(actT_e[:, b, :]), blocks(sil_e[:, b, :]),
                                     blocks(banks[2 + b][:, DE:2 * DE]), ALU.mult)

        def silu_of(act, b):
            return act.activation(blocks(sil_e[:, b, :]), blocks(banks[2 + b][:, 0:DE]), ACT.Silu)

        def weighted_a(dve, b, e):
            return dve.tensor_scalar(y_e[b][0:SLOTS, 0:512], banks[5][0:SLOTS, :], wt[0:SLOTS, bass.ds(e, 1)], None,
                                     ALU.mult)

        def weighted_b(act, b, e):
            return act.activation(y_e[b][0:SLOTS, 512:1024], banks[6][0:SLOTS, :], ACT.Copy,
                                  scale=wt[0:SLOTS, bass.ds(e, 1)])

        def pe_tables(pe, x, earlier=0):
            ps = banks[7]
            if earlier == 0:
                pe.sem_inc(x["onehot_used"], 2)
            with pe.Fori(0, NE // 8) as g:
                for b in range(2):
                    pe.wait_ge(x["onehot_done"], 2 * g + (b + 1 + NE // 4 * earlier))
                    for j in range(4):
                        for t in range(NT):
                            ins = pe.matmul(ps[:, bass.ds(g * 64 + (32 * b + 8 * j), 8)], onehot[:, b, t, j, :],
                                            vals[:, t, bass.ds(g * 8 + (4 * b + j), 1), :],
                                            start=(t == 0), stop=(t == NT - 1), skip_group_check=True)
                    ins.then_inc(x["onehot_used"], 1)

        def dve_tables(dve, link, x, earlier=0):
            with dve.Fori(0, NE // 8) as g:
                for b in range(2):
                    dve.wait_ge(x["onehot_used"], 2 * g + (b + 1 + NE // 4 * earlier))
                    for t in range(NT):
                        ins = dve.tensor_tensor(onehot[:, b, t], iota_f.unsqueeze(1).to_broadcast([P, 4, P]),
                                                place[:, t, bass.ds(g * 8 + 4 * b, 4)].unsqueeze(2).to_broadcast([P, 4, P]),
                                                ALU.is_equal)
                    ins.then_inc(x["onehot_done"], 1)
            dve.wait_ge(x["onehot_used"], NE // 4 * (earlier + 1) + 2)
            link(dve.tensor_copy(table.rearrange("p e v -> p (e v)"), banks[7][:, :]))
            link(dve.tensor_tensor(gather_f, table[:, :, 0], table[:, :, 1], ALU.add))
            link(dve.tensor_scalar(table[:, :, 7], table[:, :, 6], -FAR, FAR, ALU.mult, ALU.add))
            link(dve.scalar_tensor_tensor(out=scatter_f, in0=gather_f, scalar=float(TOPK), in1=table[:, :, 2],
                                          op0=ALU.mult, op1=ALU.add))
            link(dve.tensor_tensor(scatter_f, scatter_f, table[:, :, 7], ALU.add))
            link(dve.tensor_tensor(gather_f, gather_f, table[:, :, 7], ALU.add))
            link(dve.tensor_copy(gather_i, gather_f))
            link(dve.tensor_copy(scatter_i, scatter_f))
            link(dve.tensor_tensor(wt, table[:, :, 5], table[:, :, 4], ALU.add))
            link(dve.tensor_tensor(wt, wt, table[:, :, 3], ALU.add))
            for rows in x_g:
                link(dve.memset(rows, 0.0))
            dve.sem_inc(x["index_ready"], 1)


        def pe_experts(pe, x):
            def transpose_x(e, u):
                pe.wait_ge(x["gathered"][u], earlier_in(4, e, u, 16) + 16)
                if not is_first(e):
                    pe.wait_ge(x["xT_a"], e)
                    pe.wait_ge(x["xT_b"], e)
                rows_to_features(pe, u).then_inc(x["xtr_done"], 1)

            def gate_up(e, u):
                pe.wait_ge(x["w_in"][u], earlier_in(4, e, u, 48) + 48)
                pe.wait_ge(x["xT_a"], e + 1)
                pe.wait_ge(x["xT_b"], e + 1)
                if not is_first(e) and not is_second(e):
                    pe.wait_ge(x["act_done"], e - 1)
                gate_up_products(pe, u % 2, u).then_inc(x["gu_done"], 1)

            def down(e, u):
                pe.wait_ge(x["act_done"], e + 1)
                if not is_first(e):
                    pe.wait_ge(x["y_a"], e)
                    pe.wait_ge(x["y_b"], e)
                down_products(pe, u % 2, u).then_inc(x["y_done"], 1)

            transpose_x(0, 0)
            transpose_x(1, 1)
            gate_up(0, 0)

            def step(e, u, gate=True, rows=True):
                if gate:
                    gate_up(e + 1, (u + 1) % 4)
                if rows:
                    transpose_x(e + 2, (u + 2) % 4)
                down(e, u)

            for u in range(4):
                step(u, u)
            with pe.Fori(1, NE // 4 - 1) as g:
                for u in range(4):
                    step(4 * g + u, u)
            for u in range(4):
                step(NE - 4 + u, u, gate=u < 3, rows=u < 2)

        def act_experts(act, x):
            def silu(e, u):
                act.wait_ge(x["gu_done"], e + 1)
                if not is_first(e) and not is_second(e):
                    act.wait_ge(x["act_done"], e - 1)
                silu_of(act, u % 2).then_inc(x["sil_done"], 1)

            def x_half(e, u):
                act.wait_ge(x["xtr_done"], e + 1)
                if not is_first(e) and not is_second(e):
                    act.wait_ge(x["gu_done"], e - 1)
                act.activation(x_T[:, u % 2, 4:8, 0:SLOTS], x_copy_source(1), ACT.Copy)\
                    .then_inc(x["xT_b"], 1)

            def y_half(e, u):
                act.wait_ge(x["y_done"], e + 1)
                if not isinstance(e, int) or e >= 4:
                    act.wait_ge(x["scattered"][u], earlier_in(4, e, u, 16))
                weighted_b(act, u, e).then_inc(x["y_b"], 1)

            x_half(0, 0)
            x_half(1, 1)
            silu(0, 0)

            def step(e, u, gate=True, rows=True):
                if gate:
                    silu(e + 1, (u + 1) % 4)
                if rows:
                    x_half(e + 2, (u + 2) % 4)
                y_half(e, u)

            for u in range(4):
                step(u, u)
            with act.Fori(1, NE // 4 - 1) as g:
                for u in range(4):
                    step(4 * g + u, u)
            for u in range(4):
                step(NE - 4 + u, u, gate=u < 3, rows=u < 2)

        def dve_experts(dve, x):
            def gated(e, u):
                dve.wait_ge(x["sil_done"], e + 1)
                if not is_first(e) and not is_second(e):
                    dve.wait_ge(x["y_done"], e - 1)
                silu_product(dve, u % 2).then_inc(x["act_done"], 1)

            def x_half(e, u):
                dve.wait_ge(x["xtr_done"], e + 1)
                if not is_first(e) and not is_second(e):
                    dve.wait_ge(x["gu_done"], e - 1)
                dve.tensor_copy(x_T[:, u % 2, 0:4, 0:SLOTS], x_copy_source(0)).then_inc(x["xT_a"], 1)

            def y_half(e, u):
                dve.wait_ge(x["y_done"], e + 1)
                if not isinstance(e, int) or e >= 4:
                    dve.wait_ge(x["scattered"][u], earlier_in(4, e, u, 16))
                weighted_a(dve, u, e).then_inc(x["y_a"], 1)

            x_half(0, 0)
            x_half(1, 1)
            gated(0, 0)

            def step(e, u, gate=True, rows=True):
                if gate:
                    gated(e + 1, (u + 1) % 4)
                if rows:
                    x_half(e + 2, (u + 2) % 4)
                y_half(e, u)

            for u in range(4):
                step(u, u)
            with dve.Fori(1, NE // 4 - 1) as g:
                for u in range(4):
                    step(4 * g + u, u)
            for u in range(4):
                step(NE - 4 + u, u, gate=u < 3, rows=u < 2)

        def pool_experts(pool, link):
            x = X[0]
            bound["gather"] = pool.to_reg(TOK - 1)
            bound["scatter"] = pool.to_reg(TOK * TOPK - 1)
            pool.wait_ge(x["index_ready"], 1)
            pool.wait_ge(S["h2_out"], 16)

            def gather(e, u):
                if not isinstance(e, int) or e >= 4:
                    pool.wait_ge(x["xtr_done"], e - 3)
                pool.tensor_copy(current[:, u:u + 1], gather_i[:, bass.ds(e, 1)]).then_inc(x["index_copied"], 1)
                gather_rows(pool, x, u, copies(e, 0))

            def scatter(e, u):
                pool.wait_ge(x["y_a"], e + 1)
                pool.wait_ge(x["y_b"], e + 1)
                pool.tensor_copy(current[:, 4 + u:5 + u], scatter_i[:, bass.ds(e, 1)]).then_inc(x["index_copied"], 1)
                scatter_rows(pool, x, u, copies(e, 1))

            def copies(e, which):
                if which == 1:
                    if isinstance(e, int):
                        return min(e + 4, NE) + e + 1
                    return 2 * e + 5
                if isinstance(e, int):
                    return e + 1 + max(e - 3, 0)
                return 2 * e - 2

            for u in range(3):
                gather(u, u)

            def step(e, u, rows=True):
                if rows:
                    gather(e + 3, (u + 3) % 4)
                scatter(e, u)

            for u in range(4):
                step(u, u)
            with pool.Fori(1, NE // 4 - 1) as g:
                for u in range(4):
                    step(4 * g + u, u)
            for u in range(4):
                step(NE - 4 + u, u, rows=u < 1)
            for b in range(4):
                pool.wait_ge(x["scattered"][b], 16 * NE // 4)
            spill(pool, pool_spill)
            pool.sem_inc(S["moe_done"], 1)


        def vector_part_a(dve, link):
            link(dve.memset(mod_rows, 0.0))
            link(dve.memset(wd, 0.0))
            dve.sem_inc(S["zeroed"], 1)
            link(dve.memset(at(a_st, 4 * TOK), 0.0))
            link(dve.memset(at(a_mix + 1536, CT * conv_rows), 0.0))
            dve.wait_ge(S["sumsq"], 1)
            link(dve.tensor_scalar(stat[:, 3:6], stat[:, 0:3], 1.0 / D, EPS, ALU.mult, ALU.add))
            dve.sem_inc(S["rstd_ready"], 1)
            dve.wait_ge(S["sumsq"], 2)
            link(dve.reciprocal(stat2[:, 3:6], stat2[:, 0:3]))
            for t in range(NT):
                link(dve.tensor_scalar(xn[:, t, :], xn[:, t, :], stat2[:, 3 + t:4 + t], None, ALU.mult))
            dve.sem_inc(S["xn_ready"], 1)
            dve.wait_ge(S["consts"], 1)
            link(dve.tensor_reduce(eye32, ident.rearrange("p (q r) -> p r q", r=32), AX.X, ALU.add))
            for s in range(2):
                link(dve.tensor_scalar(sel[:, s, :], ones, eye32[:, s:s + 1], None, ALU.mult))
            dve.wait_ge(S["mod_b_in"], 16 * 8)

            def mod_bias(g):
                job = ("mod", g)
                full(dve, job)
                for q in range(4):
                    r = slice(32 * q, 32 * q + 2)
                    ins = dve.tensor_tensor(mod_rows[r, g, :], bank(job)[r, :], mod_rows[r, g, :], ALU.add)
                free(ins, job)
                drained(dve, job)

            mod_bias(0)
            dve.sem_inc(S["mod_ready"], 1)
            job = ("modT",)
            full(dve, job)
            src = bank(job)[:, :].rearrange("p (b q r) -> p q b r", b=4, q=4)
            for q in range(4):
                ins = dve.tensor_copy(modT[:, q], src[:, q, :, 0:2])
            free(ins, job)
            drained(dve, job)
            job = ("cols",)
            full(dve, job)
            ins = dve.tensor_copy(cols, bank(job)[:, 0:44])
            free(ins, job)
            drained(dve, job)
            link(dve.scalar_tensor_tensor(out=scale1, in0=modT[:, 2:4].rearrange("p q b s -> p (q b) s"), scalar=1.0,
                                          in1=cols[:, 0:8].unsqueeze(2).to_broadcast([P, KT, 2]),
                                          op0=ALU.add, op1=ALU.mult))
            dve.sem_inc(S["scale_ready"], 1)
            for k in range(0, KT, 2):
                job = ("xT", k)
                full(dve, job)
                for s, (a, b) in enumerate(((0, CTX), (CTX, TOK))):
                    ins = dve.tensor_scalar(hT[:, k, a:b], bank(job)[:, a:b], scale1[:, k, s:s + 1],
                                            modT[:, k // 4, k % 4, s:s + 1], ALU.mult, ALU.add)
                free(ins, job)
            job = ("lr",)
            full(dve, job)
            free(dve.tensor_copy(lrT[0:32, :], bank(job)[0:32, 0:TOK]), job)
            for d in range(2):
                for h in range(NH):
                    job = ("z", d, h)
                    full(dve, job)
                    free(dve.tensor_scalar(zz[:, d, h, :], bank(job)[:, 0:TOK], cols[:, 36 + 4 * d + h:37 + 4 * d + h],
                                           None, ALU.add), job)
            drained(dve, ("z", 1, NH - 1))

            zf = zz.rearrange("p a b c -> p (a b c)")
            cf = cum.rearrange("p a b c -> p (a b c)")
            dve.wait_ge(S["log_ready"], 1)
            link(dve.scalar_tensor_tensor(out=zf, in0=zf, scalar=0.0, in1=cf, op0=ALU.min, op1=ALU.subtract))
            for d in range(2):
                for h in range(NH):
                    ins = dve.tensor_tensor_scan(cum[:, d, h, :], restart, zz[:, d, h, :], 0.0, ALU.mult, ALU.add)
            link(ins)

            def chunks(f, d):
                return f[:, d].rearrange("p h (c t) -> p (h c) t", t=CHUNK)

            link(dve.tensor_copy(total, chunks(cum, 1)[:, :, CHUNK - 1]))
            link(dve.tensor_tensor(chunks(zz, 1), chunks(zz, 1), chunks(cum, 1), ALU.subtract))
            link(dve.tensor_tensor(chunks(cum, 1), chunks(zz, 1),
                                   total.unsqueeze(2).to_broadcast([P, 24, CHUNK]), ALU.add))
            for d in range(2):
                b = chunks(cum, d)
                last = b[:, :, LAST[d]:LAST[d] + 1].to_broadcast([P, 24, CHUNK])
                mid = b[:, :, MID[d]:MID[d] + 1].to_broadcast([P, 24, CHUNK])
                dve.tensor_copy(a_last[:, d, :], b[:, :, LAST[d]])
                dve.tensor_tensor(chunks(tail_f, d), last, b, ALU.subtract)
                dve.tensor_tensor(chunks(key_f, d), mid, b, ALU.subtract)
                link(dve.tensor_tensor(chunks(qry_f, d), b, mid, ALU.subtract))
                link(dve.tensor_scalar(key_f[:, d], key_f[:, d], CLAMP, None, ALU.min))
                link(dve.tensor_scalar(qry_f[:, d], qry_f[:, d], CLAMP, None, ALU.min))
                dve.sem_inc(S["last_ready"], 1)

            def rows_of(a):
                return (a[:, 0:CTX], a[:, CTX + 2:].rearrange("p (r t) -> p r t", t=GRID + 2)[:, :, 0:GRID])

            for n in range(CT):
                job = ("gc", n)
                full(dve, job)
                drained(dve, ("u", n))
                line = gated_u[:, n, :]
                dve.tensor_tensor(line[:, 1:CTX + 1], bank(job)[:, 0:CTX], u_sb[:, n, 0:CTX], ALU.mult)
                lat = line[:, CTX + 2:].rearrange("p (r t) -> p r t", t=GRID + 2)[:, :, 1:GRID + 1]
                ins = dve.tensor_tensor(lat, bank(job)[:, CTX:TOK].rearrange("p (r t) -> p r t", t=GRID),
                                        u_sb[:, n, CTX:TOK].rearrange("p (r t) -> p r t", t=GRID), ALU.mult)
                free(ins, job)
                drained(dve, job)
            for n in range(CT):
                line = gated_u[:, n, :]
                w = conv_rows - 2
                link(dve.tensor_scalar(conv_acc[:, 0:w], line[:, 1:w + 1], cols[:, 20 + n:21 + n], cols[:, 28 + n:29 + n],
                                       ALU.mult, ALU.add))
                for tap, off in ((0, 0), (2, 2)):
                    link(dve.scalar_tensor_tensor(out=conv_acc[:, 0:w], in0=line[:, off:off + w],
                                                  scalar=cols[:, 16 + 4 * tap + n:17 + 4 * tap + n],
                                                  in1=conv_acc[:, 0:w], op0=ALU.mult, op1=ALU.add))
                drained(dve, ("gb", n))
                ctx_row, lat_rows = rows_of(conv_acc)
                dve.tensor_tensor(y_conv[:, n, 0:CTX], ctx_row, gb_sb[:, n, 0:CTX], ALU.mult)
                link(dve.tensor_tensor(y_conv[:, n, CTX:TOK].rearrange("p (r t) -> p r t", t=GRID), lat_rows,
                                       gb_sb[:, n, CTX:TOK].rearrange("p (r t) -> p r t", t=GRID), ALU.mult))
            dve.sem_inc(S["conv_done"], 1)

            for d in range(2):
                for n, f in enumerate((tail_f, key_f, qry_f, cum)):
                    dve.wait_ge(S["exp_ready"], 4 * d + n + 1)
                    src, job = (kT, ("k", NH - 1)) if n < 2 else (qT, ("q", NH - 1))
                    drained(dve, job)
                    dve.tensor_tensor(f[:, d], f[:, d], src, ALU.mult).then_inc(S["fac_ready"], 1)
            dve.wait_ge(S["state_in"], 16)

            def norms(h):
                job = ("ss", h)
                full(dve, job)
                ins = dve.tensor_scalar(rms_o[:, h, :], bank(job)[:, 0:TOK], 1.0 / P, EPS, ALU.mult, ALU.add)
                free(ins, job)
                drained(dve, job)

            for h in range(NH):
                for d in range(2):
                    job = ("sc", d, h)
                    full(dve, job)
                    if h >= 2:
                        full(dve, ("o", h - 2))
                    free(dve.copy_predicated(masked[:, h % 2, d, :], mask[d], bank(job)[:, 0:TOK]), job)
                for d in range(2):
                    scan, w = SCAN[d], 4 * d + h
                    up = [bank(("up", d, h, ch % 2))[:, P * (ch // 2):P * (ch // 2) + P] for ch in scan]
                    decay = [a_last[:, d, NCH * h + ch:NCH * h + ch + 1] for ch in scan]
                    for i in range(2):
                        full(dve, ("up", d, h, i))
                    link(dve.tensor_copy(states[:, w, 0, :], up[0]))

                    def step(out, old, n):
                        return dve.scalar_tensor_tensor(out=out, in0=old, scalar=decay[n], in1=up[n],
                                                        op0=ALU.mult, op1=ALU.add)

                    link(step(new_st[:, w, :], states[:, w, 0, :], 1))
                    link(step(states[:, w, 1, :], state0[:, w, :], 2))
                    for n in (3, 4):
                        job = ("up", d, h, scan[n] % 2)
                        free(step(states[:, w, n - 1, :], states[:, w, n - 2, :], n), job)
                        drained(dve, job)
                job = ("o", h)
                full(dve, job)
                dve.wait_ge(S["sq_ready"], h + 1)
                drained(dve, ("go", h))
                ins = dve.scalar_tensor_tensor(out=y_gla[:, h, :], in0=bank(job)[:, 0:TOK], scalar=cols[:, 32 + h:33 + h],
                                               in1=y_gla[:, h, :], op0=ALU.mult, op1=ALU.mult)
                free(ins, job)
                drained(dve, job)
                if h:
                    norms(h - 1)
            dve.sem_inc(S["state_done"], 1)
            norms(NH - 1)
            dve.sem_inc(S["ro_ready"], 1)
            dve.wait_ge(S["sqrt_ready"], 1)
            link(dve.reciprocal(rms_o, rms_o))
            link(dve.tensor_tensor(y_gla, y_gla, rms_o, ALU.mult))
            dve.sem_inc(S["gla_ready"], 1)

            mod_bias(1)
            mod_bias(2)
            dve.wait_ge(S["norm2_in"], 16 * 4)
            for q in range(2):
                r = slice(32 * q, 32 * q + 2)
                link(dve.scalar_tensor_tensor(out=mod_rows[r, 2, :], in0=mod_rows[r, 2, :], scalar=1.0,
                                              in1=norm2_rows[r, :], op0=ALU.add, op1=ALU.mult))
            dve.sem_inc(S["mod_ready"], 1)
            for n in range(KT):
                job = ("mc", n)
                full(dve, job)
                drained(dve, ("gbc", n))
                ins = dve.tensor_tensor(merged[:, n, :], bank(job)[:, 0:TOK], g_conv[:, n, :], ALU.mult)
                free(ins, job)
                job = ("mg", n)
                full(dve, job)
                drained(dve, ("gbg", n))
                ins = dve.tensor_tensor(g_gla[:, n, :], bank(job)[:, 0:TOK], g_gla[:, n, :], ALU.mult)
                free(ins, job)
                drained(dve, job)
                link(dve.tensor_tensor(merged[:, n, :], merged[:, n, :], g_gla[:, n, :], ALU.add))
            dve.sem_inc(S["merged_ready"], 1)
            dve.wait_ge(S["x_again_in"], 32)
            for i in range(2):
                for t in range(NT):
                    job = ("out", i, t)
                    full(dve, job)
                    drained(dve, ("bg1", SEQ_OF[t], i))
                    part = slice(512 * i, 512 * i + 512)
                    n = NT * i + t
                    if n >= 2:
                        dve.wait_ge(S["x1_ready"], n - 1)
                    ins = dve.tensor_tensor(tmp[:, n % 2, :], bank(job)[:, :], g1_rows[:, SEQ_OF[t], part], ALU.mult)
                    free(ins, job)
                    drained(dve, job)
                    dve.tensor_tensor(x1[:, t, part], x1[:, t, part], tmp[:, n % 2, :], ALU.add).then_inc(S["x1_ready"], 1)

        def vector_part_b(dve, link):
            dve.wait_ge(S["x1_sq"], 1)
            link(dve.tensor_scalar(stat[:, 11:14], stat[:, 8:11], 1.0 / D, EPS, ALU.mult, ALU.add))
            dve.sem_inc(S["x1_sqrt"], 1)
            dve.wait_ge(S["x1_sq"], 2)
            link(dve.reciprocal(stat2[:, 11:14], stat2[:, 8:11]))
            for s in range(2):
                for i in range(2):
                    part = slice(512 * i, 512 * i + 512)
                    ja, jb = ("ba", s, i), ("bb", s, i)
                    full(dve, ja)
                    for t in range(NT):
                        if SEQ_OF[t] == s:
                            ins = dve.scalar_tensor_tensor(out=h2[:, t, part], in0=x1[:, t, part],
                                                           scalar=stat2[:, 11 + t:12 + t], in1=bank(ja)[:, :],
                                                           op0=ALU.mult, op1=ALU.mult)
                    free(ins, ja)
                    drained(dve, ja)
                    full(dve, jb)
                    for t in range(NT):
                        if SEQ_OF[t] == s:
                            ins = dve.tensor_tensor(h2[:, t, part], h2[:, t, part], bank(jb)[:, :], ALU.add)
                    free(ins, jb)
            drained(dve, ("bb", 1, 1))
            dve.sem_inc(S["h2_ready"], 1)
            for k in range(0, KT, 2):
                job = ("h2T", k)
                full(dve, job)
                free(dve.tensor_copy(hT[:, k, :], bank(job)[:, 0:TOK]), job)

            dve.wait_ge(S["router_in"], 32)
            for t in range(NT):
                drained(dve, ("r", t))
                link(dve.tensor_tensor(biased[:, t, :], scores[:, t, :], router_b, ALU.add))
                link(dve.max(top8[:, t, :], biased[:, t, :]))
                link(dve.match_replace(rest[:, t, :], top8[:, t, :], biased[:, t, :], -3e38))
            link(dve.tensor_tensor(chosen, rest, biased, ALU.not_equal))
            link(dve.tensor_copy(chosen_b, chosen))
            dve.sem_inc(S["chosen_ready"], 1)
            link(dve.tensor_tensor(scores, scores, chosen, ALU.mult))
            link(dve.tensor_reduce(weight_sum, scores, AX.X, ALU.add))
            link(dve.reciprocal(weight_sum, weight_sum))
            link(dve.scalar_tensor_tensor(out=weight, in0=scores, scalar=ROUTED_SCALE,
                                          in1=weight_sum.unsqueeze(2).to_broadcast([P, NT, NE]),
                                          op0=ALU.mult, op1=ALU.mult))
            for t in range(NT):
                ins = dve.tensor_tensor_scan(rank[:, t, :], ones[:, 0:NE], chosen[:, t, :], 0.0, ALU.mult, ALU.add)
            link(ins)
            drained(dve, ("bb", 1, 1))
            drained(dve, ("bg2", 1, 1))
            link(dve.tensor_tensor(vals[:, :, :, 2], rank, chosen, ALU.subtract))
            link(dve.tensor_copy(part_f, part_i))
            link(dve.tensor_copy(iota_f, iota_i))
            for t in range(NT):
                dve.tensor_scalar(vals[:, t, :, 0], ones[:, 0:NE], part_f[:, 0:1], None, ALU.mult)
                dve.memset(vals[:, t, :, 1], float(P * t))
            dve.memset(vals[:, :, :, 6:8], 1.0)
            link(dve.tensor_copy(vals[:, :, :, 3], weight))
            link(dve.tensor_tensor(weight, weight, vals[:, :, :, 3], ALU.subtract))
            link(dve.tensor_copy(vals[:, :, :, 4], weight))
            link(dve.tensor_tensor(weight, weight, vals[:, :, :, 4], ALU.subtract))
            link(dve.tensor_copy(vals[:, :, :, 5], weight))
            for t in range(NT):
                job = ("sgu", t)
                full(dve, job)
                dve.wait_ge(S["ssil_ready"], t + 1)
                ins = dve.tensor_tensor(act_s[:, t, :], act_s[:, t, :], bank(job)[:, DE:2 * DE], ALU.mult)
                free(ins, job)
                drained(dve, job)
            dve.sem_inc(S["ssil_ready"], NT)
            for t in range(NT):
                job = ("pos", t)
                full(dve, job)
                ins = dve.scalar_tensor_tensor(out=place[:, t, :], in0=bank(job)[:, 0:NE], scalar=1.0, in1=chosen[:, t, :],
                                               op0=ALU.add, op1=ALU.mult)
                free(ins, job)
                drained(dve, job)
            link(dve.tensor_scalar(place, place, -1.0, None, ALU.add))
            job = ("cnt",)
            full(dve, job)
            ins = dve.tensor_reduce(most_f, bank(job)[:, 0:NE], AX.X, ALU.max)
            free(ins, job)
            drained(dve, job)
            link(dve.tensor_copy(most_i, most_f))
            dve.sem_inc(S["tokens_ready"], 1)
            for t in range(NT):
                job = ("shT", t)
                full(dve, job)
                free(dve.tensor_copy(actT_s[:, t, :], bank(job)[:, 0:DE]), job)
            for job in jobs[-6:]:
                drained(dve, job)
            dve_tables(dve, link, X[0], 0)
            dve_experts(dve, X[0])
            spill(dve, dve_spill)

            for t in range(NT):
                dve.wait_ge(rows_in_sem[t], 16)
                r = rows_all[:, t]
                link(dve.tensor_tensor(r[:, 0:4, :], r[:, 0:4, :], r[:, 4:8, :], ALU.add))
                link(dve.tensor_tensor(r[:, 0:2, :], r[:, 0:2, :], r[:, 2:4, :], ALU.add))
                link(dve.tensor_tensor(r[:, 0, :], r[:, 0, :], r[:, 1, :], ALU.add))
                link(dve.tensor_tensor(r[:, 0, :], r[:, 0, :], y_shared[:, t, :], ALU.add))
                link(dve.tensor_tensor(r[:, 0, :], r[:, 0, :], g2_rows[:, SEQ_OF[t], :], ALU.mult))
                link(dve.tensor_tensor(x1[:, t, :], x1[:, t, :], r[:, 0, :], ALU.add))
                dve.sem_inc(S["routed_ready"], 1)
                dve.wait_ge(S["final_sq"], t + 1)
                link(dve.tensor_scalar(stat[:, t:t + 1], stat2[:, t:t + 1], 1.0 / D, EPS, ALU.mult, ALU.add))
                dve.sem_inc(S["routed_ready"], 1)
                dve.wait_ge(S["final_sqrt"], t + 1)
                link(dve.reciprocal(stat[:, t + 3:t + 4], stat[:, t + 6:t + 7]))
                dve.wait_ge(S["norm_w_in"], 16)
                dve.scalar_tensor_tensor(out=x1[:, t, :], in0=x1[:, t, :], scalar=stat[:, t + 3:t + 4], in1=last_w,
                                         op0=ALU.mult, op1=ALU.mult).then_inc(S["final_ready"], 1)

        block = ctx.enter_context(nc.Block())

        @block.sync
        def _(sp):
            for n, u in enumerate(units):
                if n >= UNITS:
                    old = units[n - UNITS]
                    if old[0] == "mod" and old[2] < KT - 1:
                        sp.wait_ge(S["mod_unit_used"], (KT - 1) * old[1] + old[2] + 1)
                    else:
                        full(sp, last_job(old))
                sp.dma_start(unit_view(u), unit_source(u)).then_inc(unit_in[n % UNITS], 16)
            sp.wait_ge(S["state_done"], 1)
            sp.dma_start(new_state[0, 0].rearrange("w h k v -> k (w h) v"), new_st).then_inc(S["out_done"], 16)
            sp.wait_ge(S["merged_ready"], 1)
            for n, w in enumerate((w_gate_s, w_up_s)):
                sp.dma_start(shared_w[:, n, :].rearrange("p (k f) -> p k f", k=KT),
                             w[0].rearrange("(k p) f -> p k f", p=P)).then_inc(S["shared_in"], 16)
            sp.dma_start(shared_w[:, 2, :].rearrange("p (k n) -> p k n", k=2),
                         w_down_s[0].rearrange("(k p) n -> p k n", p=P)).then_inc(S["shared_in"], 16)
            full(sp, ("out", 1, NT - 1))
            sp.wait_ge(S["out_done"], 16)
            for u in range(NXS):
                load_expert(sp, X[0], u, u)
            sp.wait_ge(S["h2_ready"], 1)
            sp.dma_start(h2_dram.rearrange("(t p) d -> p t d", p=P), h2).then_inc(S["h2_out"], 16)
            with sp.Fori(1, NE // NXS) as g:
                for u in range(NXS):
                    sp.wait_ge(X[0]["y_done"], NXS * g + (u - NXS + 1))
                    load_expert(sp, X[0], NXS * g + u, u)
            spill(sp, sp_spill)
            sp.wait_ge(S["moe_done"], 1)
            full_rows = rows_dram.rearrange("(t p k) d -> t p k d", p=P, k=TOPK)
            for t in range(NT):
                sp.dma_start(rows_all[:, t], full_rows[t]).then_inc(rows_in_sem[t], 16)
            for t in range(NT):
                sp.wait_ge(S["final_ready"], t + 1)
                dst = y_prompt[0] if t == 0 else y_sample[0, P * (t - 1):P * t, :]
                sp.dma_start(dst, x1[:, t, :]).then_inc(S["out_done"], 16)
            sp.wait_ge(S["out_done"], 16 * 4)

        @block.gpsimd
        def _(pool):
            count = [0]

            def link(ins):
                count[0] += 1
                ins.then_inc(S["pool_chain"], 1)
                pool.wait_ge(S["pool_chain"], count[0])

            link(pool.memset(ident, 0.0))
            link(pool.affine_select(out=ident, in_=ident, compare_op=ALU.not_equal, fill=1.0, base=0,
                                    pattern=[[-1, P]], channel_multiplier=1))
            link(pool.memset(ones, 1.0))
            link(pool.memset(restart, 1.0))
            rv = restart.rearrange("p (c t) -> p c t", t=CHUNK)
            link(pool.memset(rv[:, :, 0:1], 0.0))
            for d in range(2):
                link(pool.memset(mask[d], 0))
                m = mask[d].rearrange("p (t b i) -> p t b i", t=NT, b=2)
                for b in range(2):
                    link(pool.memset(m[64 * b:64 * b + 64, :, b, :], 1))
                    sign = 1 if d == 0 else -1
                    link(pool.affine_select(out=m[64 * b:64 * b + 64, :, b, :].bitcast(mybir.dt.int8),
                                            in_=m[64 * b:64 * b + 64, :, b, :].bitcast(mybir.dt.int8),
                                            compare_op=ALU.is_ge, fill=0.0, base=0,
                                            pattern=[[0, NT], [sign, CHUNK]], channel_multiplier=-sign))
            link(pool.iota(iota_i, pattern=[[1, P]], base=0, channel_multiplier=0))
            link(pool.iota(part_i, pattern=[[0, 1]], base=0, channel_multiplier=1))
            link(pool.memset(ones_b, 1.0))
            link(pool.memset(before, 1.0))
            link(pool.affine_select(out=before, in_=before, compare_op=ALU.is_gt, fill=0.0, base=0,
                                    pattern=[[1, P]], channel_multiplier=-1))
            pool.sem_inc(S["consts"], 1)
            pool_experts(pool, link)

        @block.scalar
        def _(act):
            count = [0]

            def link(ins):
                count[0] += 1
                ins.then_inc(S["act_chain"], 1)
                act.wait_ge(S["act_chain"], count[0])

            act.dma_start(scond[:, 0, :], c_ctx.rearrange("(p k) -> p k", k=KT)).then_inc(S["small_in"], 16)
            act.dma_start(scond[:, 1, :], c.rearrange("b (p k) -> (b p) k", k=KT)).then_inc(S["small_in"], 16)
            act.dma_start(xn[:, 0, :], x_prompt[0]).then_inc(S["x_in"], 16)
            act.dma_start(xn[:, 1:3, :], x_sample[0].rearrange("(t p) d -> p t d", p=P)).then_inc(S["x_in"], 16)
            loads = [(0, norm1_w[0], 8), (8, norm2_w[0], 8), (28, conv_b[0], 4)]
            for r, src, n in loads:
                act.dma_start(rows_in[r:r + n, :], src.rearrange("(r q) -> r q", q=P)).then_inc(S["small_in"], 16)
            act.dma_start(rows_in[16:28, :], conv_w[0].rearrange("w (r q) -> (w r) q", q=P)).then_inc(S["small_in"], 16)
            act.dma_start(rows_in[32:36, :], gla_norm_w[0]).then_inc(S["small_in"], 16)
            act.dma_start(rows_in[36:44, :], b_decay[0].rearrange("w (r q) -> (w r) q", q=P)).then_inc(S["small_in"], 16)
            act.dma_start(lrw, w_in0[:, C_LR:C_LR + 2 * RANK].rearrange("(k p) n -> p k n", p=P)).then_inc(S["lr_in"], 16)
            act.wait_ge(S["small_in"], 16 * 8)
            link(act.activation(scond, scond, ACT.Silu))
            act.sem_inc(S["cond_ready"], 1)
            act.wait_ge(S["zeroed"], 1)
            bm = b_mod[0].rearrange("(g q n) -> q g n", g=3, q=4)
            for q in range(4):
                for s in range(2):
                    r = 32 * q + s
                    act.dma_start(mod_rows[r:r + 1, :, :], bm[q:q + 1]).then_inc(S["mod_b_in"], 16)
            act.dma_start(wd[0:RANK, 0, :], w_decay[0, 0]).then_inc(S["wd_in"], 16)
            act.dma_start(wd[RANK:2 * RANK, 1, :], w_decay[0, 1]).then_inc(S["wd_in"], 16)
            act.wait_ge(S["x_in"], 32)
            for t in range(NT):
                link(act.activation(u_sb[:, 0:3, :].rearrange("p a b -> p (a b)")[:, 0:D], xn[:, t, :], ACT.Square,
                                    accum_out=stat[:, t:t + 1]))
            act.sem_inc(S["sumsq"], 1)
            act.wait_ge(S["rstd_ready"], 1)
            link(act.activation(stat2[:, 0:3], stat[:, 3:6], ACT.Sqrt))
            act.sem_inc(S["sumsq"], 1)
            act.dma_start(state0, state_gla[0, 0].rearrange("w h k v -> k (w h) v")).then_inc(S["state_in"], 16)
            act.dma_start(router_b, b_router.to_broadcast([P, NE])).then_inc(S["router_in"], 16)
            act.dma_start(wr, w_router[0].rearrange("(k p) n -> p k n", p=P)).then_inc(S["router_in"], 16)

            act.wait_ge(S["scale_ready"], 1)
            for k in range(1, KT, 2):
                job = ("xT", k)
                full(act, job)
                act.activation(hT[:, k, 0:CTX], bank(job)[:, 0:CTX], ACT.Identity, bias=modT[:, k // 4, k % 4, 0:1],
                               scale=scale1[:, k, 0:1])
                free(act.activation(hT[:, k, CTX:TOK], bank(job)[:, CTX:TOK], ACT.Identity,
                                    bias=modT[:, k // 4, k % 4, 1:2], scale=scale1[:, k, 1:2]), job)
            for n in range(CT):
                full(act, ("u", n))
                free(act.activation(u_sb[:, n, :], bank(("u", n))[:, 0:TOK], ACT.Copy), ("u", n))
            drained(act, ("z", 1, NH - 1))
            zf = zz.rearrange("p a b c -> p (a b c)")
            cf = cum.rearrange("p a b c -> p (a b c)")
            link(act.activation(cf, zf, ACT.Abs))
            link(act.activation(cf, cf, ACT.Exp, scale=-1.0))
            link(act.activation(cf, cf, ACT.Ln, bias=1.0))
            act.sem_inc(S["log_ready"], 1)
            for n in range(CT):
                full(act, ("gb", n))
                free(act.activation(gb_sb[:, n, :], bank(("gb", n))[:, 0:TOK], ACT.Copy), ("gb", n))
            for d in range(2):
                act.wait_ge(S["last_ready"], d + 1)
                act.activation(a_last[:, d, :], a_last[:, d, :], ACT.Exp, scale=1.0 / GATE_NORM)
                for f in (tail_f, key_f, qry_f, cum):
                    act.activation(f[:, d], f[:, d], ACT.Exp, scale=1.0 / GATE_NORM).then_inc(S["exp_ready"], 1)
            act.wait_ge(S["conv_done"], 1)
            for name, dst, scale in (("k", kT, 1.0), ("q", qT, float(P) ** -0.5)):
                for n in range(CT):
                    full(act, (name, n))
                    free(act.activation(dst[:, n, :], bank((name, n))[:, 0:TOK], ACT.Copy, scale=scale), (name, n))
            for t in range(NT):
                full(act, ("v", t))
                free(act.activation(v_sb[:, t, :], bank(("v", t))[:, :], ACT.Copy), ("v", t))
            for n in range(CT):
                full(act, ("go", n))
                free(act.activation(y_gla[:, n, :], bank(("go", n))[:, 0:TOK], ACT.Silu), ("go", n))
            for d in range(2):
                for h in range(NH):
                    full(act, ("kt", d, h))
                    free(act.activation(k_tail[:, d, h, :], bank(("kt", d, h))[:, 0:TOK], ACT.Copy), ("kt", d, h))
            for h in range(NH):
                full(act, ("o", h))
                if h >= 2:
                    act.wait_ge(bank_full[bank_of[("ss", h - 2)]], turn_of[("ss", h - 2)] + 1)
                act.activation(squares[:, h % 2, :], bank(("o", h))[:, 0:TOK], ACT.Square).then_inc(S["sq_ready"], 1)
            act.wait_ge(S["ro_ready"], 1)
            act.activation(rms_o, rms_o, ACT.Sqrt).then_inc(S["sqrt_ready"], 1)
            for name, dst in (("gbc", g_conv), ("gbg", g_gla)):
                for n in range(KT):
                    full(act, (name, n))
                    free(act.activation(dst[:, n, :], bank((name, n))[:, 0:TOK], ACT.Sigmoid), (name, n))
            act.dma_start(x1[:, 0, :], x_prompt[0]).then_inc(S["x_again_in"], 16)
            act.dma_start(x1[:, 1:3, :], x_sample[0].rearrange("(t p) d -> p t d", p=P)).then_inc(S["x_again_in"], 16)
            for q in range(2):
                for s in range(2):
                    r = 32 * q + s
                    act.dma_start(norm2_rows[r:r + 1, :], norm2_w[:, 512 * q:512 * q + 512]).then_inc(S["norm2_in"], 16)
            for s in range(2):
                for i in range(2):
                    full(act, ("bg1", s, i))
                    free(act.activation(g1_rows[:, s, 512 * i:512 * i + 512], bank(("bg1", s, i))[:, :], ACT.Copy),
                         ("bg1", s, i))
            for t in range(NT):
                act.wait_ge(S["x1_ready"], NT + t + 1)
                link(act.activation(junk, x1[:, t, :], ACT.Square,
                                    accum_out=stat[:, 8 + t:9 + t]))
            act.sem_inc(S["x1_sq"], 1)
            act.wait_ge(S["x1_sqrt"], 1)
            link(act.activation(stat2[:, 8:11], stat[:, 11:14], ACT.Sqrt))
            act.sem_inc(S["x1_sq"], 1)
            for s in range(2):
                for i in range(2):
                    full(act, ("bg2", s, i))
                    free(act.activation(g2_rows[:, s, 512 * i:512 * i + 512], bank(("bg2", s, i))[:, :], ACT.Copy),
                         ("bg2", s, i))
            for k in range(1, KT, 2):
                job = ("h2T", k)
                full(act, job)
                free(act.activation(hT[:, k, :], bank(job)[:, 0:TOK], ACT.Copy), job)
            for t in range(NT):
                job = ("r", t)
                full(act, job)
                free(act.activation(scores[:, t, :], bank(job)[:, 0:NE], ACT.Sigmoid), job)
            for t in range(NT):
                full(act, ("sgu", t))
                act.activation(act_s[:, t, :], bank(("sgu", t))[:, 0:DE], ACT.Silu).then_inc(S["ssil_ready"], 1)
            act.wait_ge(S["h2_out"], 16)
            for t in range(NT):
                for i in range(2):
                    job = ("sy", t, i)
                    full(act, job)
                    free(act.activation(y_shared[:, t, 512 * i:512 * i + 512], bank(job)[:, :], ACT.Copy), job)
            act.dma_start(last_w, final_norm_w.unsqueeze(0).to_broadcast([P, D])).then_inc(S["norm_w_in"], 16)
            act_experts(act, X[0])
            spill(act, act_spill)
            for t in range(NT):
                act.wait_ge(S["routed_ready"], 2 * t + 1)
                act.activation(y_shared[:, t, :], x1[:, t, :], ACT.Square, accum_out=stat2[:, t:t + 1])\
                    .then_inc(S["final_sq"], 1)
                act.wait_ge(S["routed_ready"], 2 * t + 2)
                act.activation(stat[:, t + 6:t + 7], stat[:, t:t + 1], ACT.Sqrt).then_inc(S["final_sqrt"], 1)

        @block.tensor
        def _(pe):
            used = [0]

            def arrived(u):
                n = unit_at[u]
                pe.wait_ge(unit_in[n % UNITS], 16 * (n // UNITS + 1))

            def start(job):
                if turn_of[job]:
                    pe.wait_ge(bank_free[bank_of[job]], turn_of[job])
                return bank(job)

            def finish(ins, job):
                ins.then_inc(bank_full[bank_of[job]], 1)

            def modulation(g):
                job = ("mod", g)
                ps = start(job)
                for k in range(KT):
                    u = ("mod", g, k)
                    arrived(u)
                    for q in range(4):
                        ins = pe.matmul(ps[32 * q:32 * q + 2, :], scond[:, :, k], unit_view(u)[:, 512 * q:512 * q + 512],
                                        start=(k == 0), stop=(k == KT - 1))
                    if k == KT - 1:
                        finish(ins, job)
                    else:
                        ins.then_inc(S["mod_unit_used"], 1)

            def project(name, ncols):
                for n in range(ncols):
                    job, u = (name, n), (name, n // 2)
                    ps = start(job)
                    arrived(u)
                    w = unit_view(u)
                    for k in range(KT):
                        ins = pe.matmul(ps[:, 0:TOK], w[:, k, P * (n % 2):P * (n % 2) + P], hT[:, k, :],
                                        start=(k == 0), stop=(k == KT - 1))
                    finish(ins, job)

            pe.wait_ge(S["cond_ready"], 1)
            modulation(0)
            pe.wait_ge(S["consts"], 1)
            pe.wait_ge(S["mod_ready"], 1)
            job = ("modT",)
            ps = start(job)
            for b in range(4):
                ins = pe.transpose(ps[:, P * b:P * b + P], mod_rows[:, 0, P * b:P * b + P], ident)
            finish(ins, job)
            job = ("cols",)
            ps = start(job)
            pe.wait_ge(S["small_in"], 16 * 8)
            finish(pe.transpose(ps[:, 0:44], rows_in[0:44, :], ident[0:44, 0:44]), job)
            pe.wait_ge(S["xn_ready"], 1)
            for k in range(KT):
                job = ("xT", k)
                ps = start(job)
                for t in range(NT):
                    ins = pe.transpose(ps[:, P * t:P * t + P], xn[:, t, P * k:P * k + P], ident)
                finish(ins, job)
            job = ("lr",)
            ps = start(job)
            pe.wait_ge(S["lr_in"], 16)
            for k in range(KT):
                drained(pe, ("xT", k))
                ins = pe.matmul(ps[0:32, 0:TOK], lrw[:, k, :], hT[:, k, :], start=(k == 0), stop=(k == KT - 1))
            finish(ins, job)
            drained(pe, ("lr",))
            pe.wait_ge(S["wd_in"], 32)
            for d in range(2):
                for h in range(NH):
                    job = ("z", d, h)
                    ps = start(job)
                    finish(pe.matmul(ps[:, 0:TOK], wd[0:32, d, P * h:P * h + P], lrT[0:32, :], start=True, stop=True), job)
            for name in ("u", "gc", "gb", "k", "q"):
                project(name, CT)
            for t in range(NT):
                job = ("v", t)
                ps = start(job)
                for i in range(2):
                    arrived(("v", i))
                    w = unit_view(("v", i))
                    for k in range(KT):
                        ins = pe.matmul(ps[:, 256 * i:256 * i + 256], hT[:, k, P * t:P * t + P], w[:, k, :],
                                        start=(k == 0), stop=(k == KT - 1))
                finish(ins, job)
            project("go", CT)

            for d in range(2):
                for h in range(NH):
                    job = ("kt", d, h)
                    ps = start(job)
                    pe.wait_ge(S["fac_ready"], 4 * d + 1)
                    for t in range(NT):
                        ins = pe.transpose(ps[:, P * t:P * t + P], tail_f[:, d, h, P * t:P * t + P], ident)
                    finish(ins, job)
            pe.wait_ge(S["fac_ready"], 8)
            pe.wait_ge(S["state_in"], 16)
            drained(pe, ("v", NT - 1))

            def sums(h):
                job = ("ss", h)
                ps = start(job)
                pe.wait_ge(S["sq_ready"], h + 1)
                finish(pe.matmul(ps[:, 0:TOK], ones, squares[:, h % 2, :], start=True, stop=True), job)

            for h in range(NH):
                for d in range(2):
                    job = ("sc", d, h)
                    ps = start(job)
                    for t in range(NT):
                        ins = pe.matmul(ps[:, P * t:P * t + P], key_f[:, d, h, P * t:P * t + P],
                                        qry_f[:, d, h, P * t:P * t + P], start=True, stop=True)
                    finish(ins, job)
                for d in range(2):
                    drained(pe, ("kt", d, h))
                    for i in range(2):
                        job = ("up", d, h, i)
                        ps = start(job)
                        for ch in sorted(ch for ch in SCAN[d][:5] if ch % 2 == i):
                            r = CHUNK * i
                            ins = pe.matmul(ps[:, P * (ch // 2):P * (ch // 2) + P],
                                            k_tail[r:r + CHUNK, d, h, P * (ch // 2):P * (ch // 2) + P],
                                            v_sb[r:r + CHUNK, ch // 2, P * h:P * h + P], start=True, stop=True)
                        finish(ins, job)
                job = ("o", h)
                ps = start(job)
                for d in range(2):
                    drained(pe, ("sc", d, h))
                    for t in range(NT):
                        pe.matmul(ps[:, P * t:P * t + P], v_sb[:, t, P * h:P * h + P],
                                  masked[:, h % 2, d, P * t:P * t + P],
                                  start=(d == 0 and t == 0), stop=False, skip_group_check=True)
                for d in range(2):
                    for i in range(2):
                        drained(pe, ("up", d, h, i))
                    scan = SCAN[d]
                    w = 4 * d + h
                    starts = [(scan[1], states[:, w, 0, :]), (scan[2], state0[:, w, :]), (scan[3], states[:, w, 1, :]),
                              (scan[4], states[:, w, 2, :]), (scan[5], states[:, w, 3, :])]
                    for n, (ch, st) in enumerate(starts):
                        ins = pe.matmul(ps[:, CHUNK * ch:CHUNK * ch + CHUNK], st,
                                        cum[:, d, h, CHUNK * ch:CHUNK * ch + CHUNK],
                                        start=False, stop=(d == 1 and n == 4), skip_group_check=True)
                finish(ins, job)
                if h:
                    sums(h - 1)
            sums(NH - 1)
            project("gbc", KT)
            project("gbg", KT)
            for g in (1, 2):
                modulation(g)
            pe.wait_ge(S["mod_ready"], 2)
            for s in range(2):
                for i in range(2):
                    job = ("bg1", s, i)
                    ps = start(job)
                    finish(pe.matmul(ps[:, :], sel[32 * i:32 * i + 2, s, :], mod_rows[32 * i:32 * i + 2, 1, :],
                                     start=True, stop=True), job)
            pe.wait_ge(S["gla_ready"], 1)
            for n in range(KT):
                for name, y in (("c", y_conv), ("g", y_gla)):
                    job, u = ("m" + name, n), ("wb" + name, n // 4)
                    ps = start(job)
                    arrived(u)
                    w = unit_view(u)
                    for k in range(CT):
                        ins = pe.matmul(ps[:, 0:TOK], w[:, k, P * (n % 4):P * (n % 4) + P], y[:, k, :],
                                        start=(k == 0), stop=(k == CT - 1))
                    finish(ins, job)
            pe.wait_ge(S["merged_ready"], 1)
            for i in range(2):
                for t in range(NT):
                    job = ("out", i, t)
                    ps = start(job)
                    for j in range(2):
                        u = ("wo", 2 * i + j)
                        arrived(u)
                        w = unit_view(u)
                        for k in range(KT):
                            ins = pe.matmul(ps[:, 256 * j:256 * j + 256], merged[:, k, P * t:P * t + P], w[:, k, :],
                                            start=(k == 0), stop=(k == KT - 1))
                    finish(ins, job)
            for s in range(2):
                for i in range(2):
                    job = ("bg2", s, i)
                    ps = start(job)
                    r = 32 * (2 + i)
                    finish(pe.matmul(ps[:, :], sel[r:r + 2, s, :], mod_rows[r:r + 2, 2, :], start=True, stop=True), job)
            for s in range(2):
                for i in range(2):
                    job = ("ba", s, i)
                    ps = start(job)
                    r = 32 * i
                    finish(pe.matmul(ps[:, :], sel[r:r + 2, s, :], mod_rows[r:r + 2, 2, :], start=True, stop=True), job)
                    job = ("bb", s, i)
                    ps = start(job)
                    r = 32 * (2 + i)
                    finish(pe.matmul(ps[:, :], sel[r:r + 2, s, :], mod_rows[r:r + 2, 1, :], start=True, stop=True), job)
            pe.wait_ge(S["h2_ready"], 1)
            for k in range(KT):
                job = ("h2T", k)
                ps = start(job)
                for t in range(NT):
                    ins = pe.transpose(ps[:, P * t:P * t + P], h2[:, t, P * k:P * k + P], ident)
                finish(ins, job)
            for k in (KT - 2, KT - 1):
                drained(pe, ("h2T", k))
            pe.wait_ge(S["router_in"], 32)
            for t in range(NT):
                job = ("r", t)
                ps = start(job)
                for k in range(KT):
                    ins = pe.matmul(ps[:, 0:NE], hT[:, k, P * t:P * t + P], wr[:, k, :], start=(k == 0), stop=(k == KT - 1))
                finish(ins, job)
            pe.wait_ge(S["shared_in"], 48)
            for t in range(NT):
                job = ("sgu", t)
                ps = start(job)
                for k in range(KT):
                    ins = pe.matmul(ps[:, :], hT[:, k, P * t:P * t + P],
                                    shared_w[:, 0:2, DE * k:DE * k + DE], start=(k == 0), stop=(k == KT - 1))
                finish(ins, job)
            pe.wait_ge(S["chosen_ready"], 1)
            for t in range(NT):
                job = ("pos", t)
                ps = start(job)
                for u in range(t):
                    pe.matmul(ps[:, 0:NE], ones_b, chosen_b[:, u, :], start=(u == 0), stop=False)
                finish(pe.matmul(ps[:, 0:NE], before, chosen_b[:, t, :], start=(t == 0), stop=True), job)
            job = ("cnt",)
            ps = start(job)
            for t in range(NT):
                ins = pe.matmul(ps[:, 0:NE], ones_b, chosen_b[:, t, :], start=(t == 0), stop=(t == NT - 1))
            finish(ins, job)
            for t in range(NT):
                job = ("shT", t)
                ps = start(job)
                pe.wait_ge(S["ssil_ready"], NT + t + 1)
                for k in range(2):
                    ins = pe.transpose(ps[:, P * k:P * k + P], act_s[:, t, P * k:P * k + P], ident)
                finish(ins, job)
            for t in range(NT):
                drained(pe, ("shT", t))
                for i in range(2):
                    job = ("sy", t, i)
                    ps = start(job)
                    for k in range(2):
                        ins = pe.matmul(ps[:, :], actT_s[:, t, P * k:P * k + P],
                                        shared_w[:, 2, D * k + 512 * i:D * k + 512 * i + 512], start=(k == 0), stop=(k == 1))
                    finish(ins, job)
            for job in jobs[-8:]:
                drained(pe, job)
            pe_tables(pe, X[0])
            pe_experts(pe, X[0])
            spill(pe, pe_spill)

        @block.vector
        def _(dve):
            count = [0]

            def link(ins):
                count[0] += 1
                ins.then_inc(S["dve_chain"], 1)
                dve.wait_ge(S["dve_chain"], count[0])

            vector_part_a(dve, link)
            vector_part_b(dve, link)


_INS = ["x_prompt", "x_sample", "state_gla", "c", "c_ctx", "w_mod", "b_mod", "norm1_w", "w_in", "conv_w", "conv_b",
        "w_decay", "b_decay", "gla_norm_w", "w_br_conv", "w_br_gla", "w_out", "norm2_w", "w_router", "b_router",
        "w_gate_e", "w_up_e", "w_down_e", "w_gate_s", "w_up_s", "w_down_s", "final_norm_w"]
_OUTS = [((1, CTX, D), "float32"), ((1, LAT, D), "float32"), ((1, 1, 2, NH, P, P), "float32")]


def kernel(**inputs):
    import numpy as _np
    import concourse.bacc as _bacc
    from concourse import mybir as _mybir
    from concourse.bass_utils import run_bass_kernel_spmd as _run

    nc = _bacc.Bacc("TRN2", target_bir_lowering=False, num_devices=1)
    arrays, args = {}, []
    for name in _INS:
        a = _np.ascontiguousarray(inputs[name])
        arrays[f"in_{name}_dram"] = a
        args.append(nc.dram_tensor(f"in_{name}_dram", a.shape, _mybir.dt.from_np(a.dtype), kind="ExternalInput").ap())
    for i, (shape, dtype) in enumerate(_OUTS):
        dt = _mybir.dt.from_np(_np.dtype(dtype))
        args.append(nc.dram_tensor(f"out_{i}_dram", shape, dt, kind="ExternalOutput").ap())
    program(nc, *args)
    r = _run(nc, [arrays], core_ids=[0])
    return tuple(r.results[0][f"out_{i}_dram"] for i in range(len(_OUTS)))
```
